# Optimizing a Trainium2 kernel written in Bass

```python
import math
import jax, jax.numpy as jnp
from jax import lax
import numpy as np

D_MODEL = 1024
BATCH = 1
SEQ = 1024
DEPTH = 1

CTX_LEN = 256
GRID_W = 64
MIX_W = D_MODEL
GDN_W = MIX_W // 2
SGU_W = MIX_W - GDN_W
HEAD_DIM = 128
GDN_HEADS = GDN_W // HEAD_DIM
SGU_GROUP = 128
SGU_GROUPS = SGU_W // SGU_GROUP
SGU_CHUNK = 128
DELTA_CHUNK = 64
CONV_W = 3
N_EXPERTS = 32
TOP_K = 4
D_FF = D_MODEL
SWIGLU_LIMIT = 7.0
SWIGLU_ALPHA = 1.702
MOE_BLOCK = 128
NORM_EPS = 1e-6

QKV_COLS = 3 * GDN_W
STATE_COLS = QKV_COLS + 4 * GDN_HEADS
Z_END = STATE_COLS + GDN_W
U_END = Z_END + SGU_W
PROJ_COLS = U_END + SGU_W

kernel_name = "hybrid_gdn_sgu_moe_prefix_dit"

def _rmsnorm(x, g):
    x32 = x.astype(jnp.float32)
    y = x32 * lax.rsqrt(jnp.mean(x32 * x32, -1, keepdims=True) + NORM_EPS)
    return (y * g.astype(jnp.float32)).astype(x.dtype)

def _layernorm(x, g, b):
    x32 = x.astype(jnp.float32)
    xc = x32 - jnp.mean(x32, -1, keepdims=True)
    y = xc * lax.rsqrt(jnp.mean(xc * xc, -1, keepdims=True) + NORM_EPS)
    return (y * g + b).astype(x.dtype)

def _l2norm(x):
    x32 = x.astype(jnp.float32)
    return x32 * lax.rsqrt(jnp.sum(x32 * x32, -1, keepdims=True) + NORM_EPS)

def _dwconv_centred(x, w):
    pad = CONV_W // 2
    L = x.shape[-2]
    xp = jnp.pad(x, [(0, 0)] * (x.ndim - 2) + [(pad, pad), (0, 0)])
    return sum(xp[..., j:j + L, :] * w[j] for j in range(CONV_W))

def _state_step(s, u_i, w_i, kd_i, gl_i):
    v_new = u_i - jnp.einsum('bhck,bhkv->bhcv', w_i, s)
    s_next = s * gl_i[..., None, None] + jnp.einsum('bhck,bhcv->bhkv', kd_i, v_new)
    return s_next, v_new

def _chunk_gated_delta(q, k, v, g, beta, s0, need_out):
    B, H, L, Dk = q.shape
    Dv = v.shape[-1]
    C = DELTA_CHUNK
    N = L // C
    q = q.reshape(B, H, N, C, Dk)
    k = k.reshape(B, H, N, C, Dk)
    v = v.reshape(B, H, N, C, Dv)
    g = jnp.cumsum(g.reshape(B, H, N, C), -1)
    beta = beta.reshape(B, H, N, C)
    incl = jnp.tril(jnp.ones((C, C), bool))
    strict = jnp.tril(jnp.ones((C, C), bool), -1)
    decay = jnp.where(incl, jnp.exp(jnp.where(incl, g[..., :, None] - g[..., None, :], 0.0)), 0.0)
    kb = k * beta[..., None]
    a = jnp.where(strict, jnp.einsum('bhnid,bhnjd->bhnij', kb, k) * decay, 0.0)
    eye = jnp.eye(C, dtype=q.dtype)
    t_inv = lax.linalg.triangular_solve(eye + a, jnp.broadcast_to(eye, a.shape), left_side=True,
                                        lower=True, unit_diagonal=True)
    u = jnp.einsum('bhnij,bhnjd->bhnid', t_inv, v * beta[..., None])
    w = jnp.einsum('bhnij,bhnjd->bhnid', t_inv, kb * jnp.exp(g)[..., None])
    k_dec = k * jnp.exp(g[..., -1:] - g)[..., None]
    g_last = jnp.exp(g[..., -1])
    to_scan = lambda t: jnp.moveaxis(t, 2, 0)
    if need_out:
        attn = jnp.where(incl, jnp.einsum('bhnid,bhnjd->bhnij', q, k) * decay, 0.0)
        q_dec = q * jnp.exp(g)[..., None]

        def step(s, xs):
            u_i, w_i, kd_i, gl_i, qd_i, at_i = xs
            s_next, v_new = _state_step(s, u_i, w_i, kd_i, gl_i)
            o = jnp.einsum('bhck,bhkv->bhcv', qd_i, s) + jnp.einsum('bhij,bhjv->bhiv', at_i, v_new)
            return s_next, o

        s, o = lax.scan(step, s0, tuple(map(to_scan, (u, w, k_dec, g_last, q_dec, attn))))
        return jnp.moveaxis(o, 0, 2).reshape(B, H, L, Dv), s

    def step_state(s, xs):
        s_next, _ = _state_step(s, *xs)
        return s_next, None

    s, _ = lax.scan(step_state, s0, tuple(map(to_scan, (u, w, k_dec, g_last))))
    return None, s

def _gdn_prepare(p, conv_w, a_log, dt_bias, rows):
    B, L, _ = p.shape
    qkv = p[..., :QKV_COLS].reshape(B, rows, L // rows, QKV_COLS)
    qkv = jax.nn.silu(_dwconv_centred(qkv, conv_w)).astype(jnp.float32)
    qkv = qkv.reshape(B, L, 3, GDN_HEADS, HEAD_DIM).transpose(2, 0, 3, 1, 4)
    q = _l2norm(qkv[0]) * (HEAD_DIM ** -0.5)
    k = _l2norm(qkv[1])
    v = qkv[2]
    ba = p[..., QKV_COLS:STATE_COLS].astype(jnp.float32).reshape(B, L, 2, 2, GDN_HEADS)
    ba = ba.transpose(2, 3, 0, 4, 1)
    beta = jax.nn.sigmoid(ba[0])
    g = -jnp.exp(a_log)[:, None, :, None] * jax.nn.softplus(ba[1] + dt_bias[:, None, :, None])
    return q, k, v, g, beta

def _gdn_bidir(q, k, v, g, beta, s0, need_out):
    flip = lambda t: jnp.flip(t, axis=2)
    o_f, s_f = _chunk_gated_delta(q, k, v, g[0], beta[0], s0[0], need_out)
    o_b, s_b = _chunk_gated_delta(flip(q), flip(k), flip(v), flip(g[1]), flip(beta[1]), s0[1], need_out)
    o = o_f + flip(o_b) if need_out else None
    return o, jnp.stack([s_f, s_b])

def _gdn_output(o, z, norm_g):
    B, H, L, Dv = o.shape
    o = o.transpose(0, 2, 1, 3)
    zz = z.reshape(B, L, H, Dv).astype(jnp.float32)
    o = o * lax.rsqrt(jnp.mean(o * o, -1, keepdims=True) + NORM_EPS) * norm_g * jax.nn.silu(zz)
    return o.reshape(B, L, GDN_W).astype(z.dtype)

def _sgu(p, ln_g, ln_b, w_s, b_s):
    B, L, _ = p.shape
    shp = (B, L // SGU_CHUNK, SGU_CHUNK, SGU_GROUPS, SGU_GROUP)
    u = jax.nn.gelu(p[..., Z_END:U_END]).reshape(shp)
    v = _layernorm(jax.nn.gelu(p[..., U_END:PROJ_COLS]).reshape(shp), ln_g, ln_b)
    s = jnp.einsum('gpq,bnqgc->bnpgc', w_s, v) + b_s.T[:, :, None]
    return (u * s).reshape(B, L, SGU_W)

def _moe(h, router_w, router_b, w_gu, b_gu, w_down, b_down):
    T, D = h.shape
    logits = (h @ router_w + router_b).astype(jnp.float32)
    top_v, top_i = lax.top_k(logits, TOP_K)
    gates = jax.nn.softmax(top_v, axis=-1).astype(h.dtype)
    n_assign = T * TOP_K
    flat_e = top_i.reshape(-1)
    order = jnp.argsort(flat_e)
    e_sorted = flat_e[order]
    tok_sorted = (order // TOP_K).astype(jnp.int32)
    gate_sorted = gates.reshape(-1)[order]
    counts = jnp.bincount(flat_e, length=N_EXPERTS)
    padded = (counts + MOE_BLOCK - 1) // MOE_BLOCK * MOE_BLOCK
    pad_end = jnp.cumsum(padded)
    dest = ((pad_end - padded)[e_sorted] + jnp.arange(n_assign)
            - (jnp.cumsum(counts) - counts)[e_sorted])
    n_blocks = -(-n_assign // MOE_BLOCK) + N_EXPERTS
    slot_tok = jnp.full((n_blocks * MOE_BLOCK,), T, jnp.int32).at[dest].set(tok_sorted)
    block_e = jnp.minimum(jnp.searchsorted(pad_end, jnp.arange(n_blocks) * MOE_BLOCK, side='right'),
                          N_EXPERTS - 1)
    xb = jnp.concatenate([h, jnp.zeros((1, D), h.dtype)])[slot_tok].reshape(n_blocks, MOE_BLOCK, D)

    def expert_block(args):
        xblk, e = args
        gu = xblk @ w_gu[e] + b_gu[e]
        gate = jnp.minimum(gu[:, ::2], SWIGLU_LIMIT)
        up = jnp.clip(gu[:, 1::2], -SWIGLU_LIMIT, SWIGLU_LIMIT)
        act = (up + 1.0) * gate * jax.nn.sigmoid(SWIGLU_ALPHA * gate)
        return act @ w_down[e] + b_down[e]

    yb = lax.map(expert_block, (xb, block_e))
    y = yb.reshape(-1, D)[dest] * gate_sorted[:, None]
    return jnp.zeros_like(h).at[tok_sorted].add(y)

def setup_inputs(seed: int = 0) -> dict:
    key = jax.random.key(seed)
    ks = jax.random.split(key, 24)
    D = D_MODEL
    nrm = lambda k, shape, s: jax.random.normal(k, shape, jnp.float32) * s
    dt = jnp.exp(jax.random.uniform(ks[10], (DEPTH, 2, GDN_HEADS), jnp.float32,
                                    minval=math.log(1e-3), maxval=math.log(1e-1)))
    return {
        "x": nrm(ks[0], (BATCH, SEQ, D), 1.0),
        "c": nrm(ks[1], (BATCH, D), 1.0),
        "ctx": nrm(ks[2], (BATCH, CTX_LEN, D), 1.0),
        "c_ctx": nrm(ks[3], (D,), 1.0),
        "w_ada": nrm(ks[4], (DEPTH, D, 6 * D), D ** -0.5),
        "b_ada": nrm(ks[5], (DEPTH, 6 * D), 0.02),
        "norm_g": 1.0 + nrm(ks[6], (DEPTH, 4, D), 0.05),
        "w_in": nrm(ks[7], (DEPTH, D, PROJ_COLS), D ** -0.5),
        "conv_w": nrm(ks[8], (DEPTH, CONV_W, QKV_COLS), CONV_W ** -0.5),
        "a_log": jnp.log(jax.random.uniform(ks[9], (DEPTH, 2, GDN_HEADS), jnp.float32, minval=1.0, maxval=16.0)),
        "dt_bias": dt + jnp.log(-jnp.expm1(-dt)),
        "gdn_norm_g": 1.0 + nrm(ks[11], (DEPTH, HEAD_DIM), 0.05),
        "sgu_ln_g": 1.0 + nrm(ks[12], (DEPTH, SGU_GROUPS, SGU_GROUP), 0.05),
        "sgu_ln_b": nrm(ks[13], (DEPTH, SGU_GROUPS, SGU_GROUP), 0.02),
        "sgu_w": nrm(ks[14], (DEPTH, SGU_GROUPS, SGU_CHUNK, SGU_CHUNK), SGU_CHUNK ** -0.5),
        "sgu_b": 1.0 + nrm(ks[15], (DEPTH, SGU_GROUPS, SGU_CHUNK), 0.1),
        "w_out": nrm(ks[16], (DEPTH, MIX_W, D), MIX_W ** -0.5),
        "router_w": nrm(ks[17], (DEPTH, D, N_EXPERTS), D ** -0.5),
        "router_b": nrm(ks[18], (DEPTH, N_EXPERTS), 0.01),
        "w_gu": nrm(ks[19], (DEPTH, N_EXPERTS, D, 2 * D_FF), D ** -0.5),
        "b_gu": nrm(ks[20], (DEPTH, N_EXPERTS, 2 * D_FF), 0.02),
        "w_down": nrm(ks[21], (DEPTH, N_EXPERTS, D_FF, D), D_FF ** -0.5),
        "b_down": nrm(ks[22], (DEPTH, N_EXPERTS, D), 0.02),
    }

def reference(x, c, ctx, c_ctx, w_ada, b_ada, norm_g, w_in, conv_w, a_log, dt_bias, gdn_norm_g,
              sgu_ln_g, sgu_ln_b, sgu_w, sgu_b, w_out, router_w, router_b, w_gu, b_gu, w_down, b_down):
    B, L, D = x.shape
    rows = L // GRID_W
    xc = ctx
    for layer in range(DEPTH):
        last = layer == DEPTH - 1
        mod = (jax.nn.silu(c) @ w_ada[layer] + b_ada[layer]).reshape(B, 6, 1, D)
        mod_c = (jax.nn.silu(c_ctx) @ w_ada[layer] + b_ada[layer]).reshape(6, 1, 1, D)
        ng = norm_g[layer]

        h = _rmsnorm(x, ng[0]) * (1.0 + mod[:, 1]) + mod[:, 0]
        hc = _rmsnorm(xc, ng[0]) * (1.0 + mod_c[1]) + mod_c[0]
        p = h @ w_in[layer]
        pc = hc @ (w_in[layer][:, :STATE_COLS] if last else w_in[layer])

        qc, kc, vc, gcx, bcx = _gdn_prepare(pc, conv_w[layer], a_log[layer], dt_bias[layer], 1)
        s_zero = jnp.zeros((2, B, GDN_HEADS, HEAD_DIM, HEAD_DIM), jnp.float32)
        oc, s_ctx = _gdn_bidir(qc, kc, vc, gcx, bcx, s_zero, not last)

        q, k, v, g, beta = _gdn_prepare(p, conv_w[layer], a_log[layer], dt_bias[layer], rows)
        o, _ = _gdn_bidir(q, k, v, g, beta, s_ctx, True)
        mix = jnp.concatenate([
            _gdn_output(o, p[..., STATE_COLS:Z_END], gdn_norm_g[layer]),
            _sgu(p, sgu_ln_g[layer], sgu_ln_b[layer], sgu_w[layer], sgu_b[layer])], axis=-1)
        x = x + mod[:, 2] * _rmsnorm(mix @ w_out[layer], ng[1])
        if not last:
            mix_c = jnp.concatenate([
                _gdn_output(oc, pc[..., STATE_COLS:Z_END], gdn_norm_g[layer]),
                _sgu(pc, sgu_ln_g[layer], sgu_ln_b[layer], sgu_w[layer], sgu_b[layer])], axis=-1)
            xc = xc + mod_c[2] * _rmsnorm(mix_c @ w_out[layer], ng[1])

        h = (_rmsnorm(x, ng[2]) * (1.0 + mod[:, 4]) + mod[:, 3]).reshape(-1, D)
        if not last:
            hc = (_rmsnorm(xc, ng[2]) * (1.0 + mod_c[4]) + mod_c[3]).reshape(-1, D)
            h = jnp.concatenate([h, hc], axis=0)
        y = _moe(h, router_w[layer], router_b[layer], w_gu[layer], b_gu[layer], w_down[layer], b_down[layer])
        x = x + mod[:, 5] * _rmsnorm(y[:B * L].reshape(B, L, D), ng[3])
        if not last:
            xc = xc + mod_c[5] * _rmsnorm(y[B * L:].reshape(xc.shape), ng[3])
    return x


_drawn_inputs = setup_inputs


def setup_inputs(seed=0):
    import zlib

    import numpy as np

    out = dict(_drawn_inputs(seed))
    spreads = {}
    factors = {'sgu_ln_b': 2.713, 'b_gu': 6.06, 'b_down': 8.0}
    for name, (base, spread) in spreads.items():
        noise = np.random.default_rng([zlib.crc32(name.encode()), seed]).standard_normal(out[name].shape)
        drawn = base * np.exp(spread * noise) if base else spread * noise
        out[name] = __import__('jax').numpy.asarray(drawn.astype(out[name].dtype))
    for name, factor in factors.items():
        out[name] = (out[name] * factor).astype(out[name].dtype)
    return out
```

```python
import concourse.bass as bass
from concourse import mybir
from concourse.alu_op_type import AluOpType as ALU
from contextlib import ExitStack

F32 = mybir.dt.float32
BF16 = mybir.dt.bfloat16
I32 = mybir.dt.int32
U32 = mybir.dt.uint32
ACT = mybir.ActivationFunctionType
AX = mybir.AxisListType

P = 128
D = 1024
KD = D // P
SEQ, CTX = 1024, 256
NT = SEQ // P
NC = CTX // P
NA = NT + NC
TOK = SEQ + CTX
H = 4
DIRS = 2
ROW = 64
NE, TOPK = 32, 4
QKV = 3 * H * P
BA = 4 * H
Z0 = QKV + BA
U0 = Z0 + H * P
V0 = U0 + H * P
NADA = 6 * D // 512
EPS = 1e-6
HUGE = 1e30
LIMIT, ALPHA = 7.0, 1.702
LINKS = {False: 6, True: 8}
LEVELS = 7
MAXB = SEQ * TOPK // P + NE - 1
SLOT = KD * 512


class Link:

    def __init__(self, eng, sem):
        self.eng, self.sem, self.n, self.base = eng, sem, 0, 0

    def __call__(self, ins):
        ins.then_inc(self.sem, 1)
        self.n += 1
        self.eng.wait_ge(self.sem, self.base + self.n)

    def turn(self, t, per):
        self.start, self.per, self.before = self.n, per, self.base
        self.base = t * per + (self.before + self.start)
        self.n = 0

    def end(self, turns):
        assert self.n == self.per, (self.n, self.per)
        self.base, self.n = self.before + self.start + turns * self.per, 0


class Event:

    def __init__(self, sem, per):
        self.sem, self.per = sem, per

    def ahead(self, eng):
        eng.sem_inc(self.sem, self.per)

    def now(self, eng, s, j):
        eng.wait_ge(self.sem, s * self.per + (self.per + j + 1))

    def before(self, eng, s, j):
        eng.wait_ge(self.sem, s * self.per + (j + 1))


def hybrid_block(nc, x, c, ctx_in, c_ctx, w_ada, b_ada, norm_g, w_in, conv_w, a_log, dt_bias,
                 gdn_norm_g, sgu_ln_g, sgu_ln_b, sgu_w, sgu_b, w_out, router_w, router_b,
                 w_gu, b_gu, w_down, b_down, out, dbg=None):
    es = ExitStack()
    with es:
        def sb(name, shape, dt=F32):
            return es.enter_context(nc.sbuf_tensor(name, shape, dt))

        def sem(name):
            return es.enter_context(nc.semaphore(name))

        W = sb("weights", [P, 6 * SLOT])
        HT = sb("hT", [P, KD * TOK])
        QK = sb("qkv", [P, 3 * H * TOK])
        hT = HT[:].rearrange("p (k t) -> p k t", k=KD)
        qkvT = QK[:].rearrange("p (c t) -> p c t", c=3 * H)

        def slot(i):
            return W[:, i * SLOT:(i + 1) * SLOT]

        zs = slot(3).rearrange("p (n c) -> p n c", n=NT)
        uT = slot(4).rearrange("p (g t) -> p g t", g=H)
        o_acc = slot(5).rearrange("p (n c) -> p n c", n=NT)
        st5 = slot(5).rearrange("p (b c) -> p b c", b=8)
        v_gelu, v_norm, conv_in, conv_out = st5[:, 0:2], st5[:, 2:4], st5[:, 4:6], st5[:, 6:8]
        xs = QK[:, 0:4 * D].rearrange("p (b d) -> p b d", b=4)
        junk = QK[:, 4 * D:5 * D]
        tail = QK[:, 2 * H * TOK:]
        sguT = tail[:, 0:512].rearrange("p (g q) -> p g q", g=H)
        sgu_raw = tail[:, 512:1024].rearrange("p (g q) -> p g q", g=H)
        sgu_bb, ln_gb, ln_bb = tail[:, 1024:1536], tail[:, 1536:2048], tail[:, 2048:2560]

        ident = sb("ident", [P, P])
        ones = sb("ones", [P, P])
        tri = sb("tri", [P, DIRS, P])
        zmask = sb("zmask", [P, DIRS, P])
        same = sb("same", [P, LEVELS - 1, P])
        neg0 = sb("neg0", [P, P])
        cols = sb("cols", [P, 96])
        ccol = sb("ccol", [P, 3 * 12])
        cs = sb("cs", [P, KD, 2])
        modc = sb("modc", [P, 48, 2])
        scA = sb("scA", [P, 2, KD])
        sc2 = sb("sc2", [P, KD])
        gvec = sb("gvec", [P, 2, KD])
        wba = sb("wba", [P, KD, BA])
        ba = sb("ba", [P, NA, BA])
        beta = sb("beta", [P, NA, 8])
        gdec = sb("gdec", [P, NA, 8])
        batmp = sb("batmp", [P, NA, 8])
        alog = sb("alog", [P, 8])
        dtb = sb("dtb", [P, 8])
        ssq = sb("ssq", [P, 16])
        rst = sb("rst", [P, 16])
        stat = sb("stat", [P, H, 6])
        mv = sb("mv", [P, H, 2])
        lrs = sb("lrs", [P, H])
        eps_c = sb("eps_c", [P, 1])
        mhalf = sb("mhalf", [P, 8])
        gng = sb("gng", [P, P])
        rows = ident_rows = QK[:, 5 * D:5 * D + 384].rearrange("p (a b) -> p a b", a=3)
        modrow = QK[:, 6 * D:6 * D + 1024].rearrange("p (a b) -> p a b", a=2)
        idx_i = sb("idx_i", [P, 8], I32)
        idx_f = sb("idx_f", [P, 8])

        def carve(region, sizes):
            at, parts = 0, []
            for n in sizes:
                parts.append(region[:, at:at + n])
                at += n
            assert at <= region.shape[1], at
            return parts

        (xr, on, mixT, x1, xn2, g1row, junk2, h2T) = carve(QK[:], [2 * D, 2 * 512, 2 * 512, 2 * D, 2 * D, D, D, 2 * D])
        xr, x1, xn2 = (a.rearrange("p (b d) -> p b d", b=2) for a in (xr, x1, xn2))
        on = on.rearrange("p (b c) -> p b c", b=2)
        mixT = mixT.rearrange("p (b k t) -> p b k t", b=2, k=H)
        h2T = h2T.rearrange("p (b k t) -> p b k t", b=2, k=KD)
        b_raw, b_part = carve(QK[:, 12 * D:], [512, 768])
        b_part = b_part.bitcast(BF16).rearrange("p (j c) -> p j c", j=3)
        wo = [HT[:, i * SLOT:(i + 1) * SLOT].rearrange("p (k n) -> p k n", k=KD) for i in range(2)]
        (rw, rb, oneh, chosen, top, dests, gates, base, slotf, blkf) = carve(
            HT[:, 2 * SLOT:], [KD * NE, NE, NT * TOPK * NE, NT * NE, NT * 8, NT * TOPK, NT * TOPK, NE, 32, 32])
        rw = rw.rearrange("p (k e) -> p k e", k=KD)
        oneh = oneh.rearrange("p (n k e) -> p n k e", n=NT, k=TOPK)
        chosen = chosen.rearrange("p (n e) -> p n e", n=NT)
        top = top.rearrange("p (n k) -> p n k", n=NT)
        dests, gates = (a.rearrange("p (n k) -> p n k", n=NT) for a in (dests, gates))
        (xg, xT, act_n, gate_n, up_n, sig_n, actT, ysb, bias3, onesb) = carve(
            QK[:], [D, D, 512, 512, 512, 512, D, D, D, 64])
        act_n, gate_n, up_n, sig_n = (a.rearrange("p (b c) -> p b c", b=2) for a in (act_n, gate_n, up_n, sig_n))
        xT = xT.rearrange("p (k t) -> p k t", k=KD)
        actT = actT.rearrange("p (k t) -> p k t", k=KD)
        bias3 = bias3.bitcast(BF16)
        onesb = onesb.bitcast(BF16)
        bdn = QK[:, 8 * D:9 * D]
        (g2row, mixe, x1r, acc, junk3, gT) = carve(QK[:, 9 * D:], [D, NT * NE, 2 * D, D, D, 128])
        mixe = mixe.rearrange("p (n e) -> p n e", n=NT)
        x1r = x1r.rearrange("p (b d) -> p b d", b=2)
        yg = HT[:, 0:8 * D].rearrange("p (b k d) -> p b k d", b=2, k=TOPK)
        iota = sb("iota", [P, P])
        tokid = sb("tokid", [P, NT])
        top_i = sb("top_i", [P, 8], U32)
        top_f = sb("top_f", [P, 8])
        strict = sb("strict", [NE, NE])
        nbi = sb("nbi", [NE, 1], I32)
        nbf = sb("nbf", [NE, 1])
        endf = sb("endf", [NE, 1])
        (meta_f, meta, past, slots, dest_i, tmp_i) = carve(QK[:, 14720:], [192, 192, 64, 64, NT * TOPK, NT * TOPK])
        meta_f, meta, past = meta_f[0:1, :], meta[0:1, :].bitcast(I32), past[0:NE, :]
        slots = slots.bitcast(U32)
        dest_i, tmp_i = dest_i.bitcast(I32), tmp_i.bitcast(I32)
        idx = sb("idx", [P, 1], U32)
        hotS, hotB = carve(HT[:, D:2 * D], [2 * P, 2 * 64])
        hotS, hotB = hotS.rearrange("p (b c) -> p b c", b=2), hotB.rearrange("p (b c) -> p b c", b=2)
        x1_d = nc.dram_tensor("x1_scratch", (SEQ, D), F32, kind="Internal").ap()
        xn_d = nc.dram_tensor("xn_scratch", (SEQ, D), F32, kind="Internal").ap()
        y_d = nc.dram_tensor("y_scratch", (64 * P, D), F32, kind="Internal").ap()
        b3_d = nc.dram_tensor("b_gu_parts", (3, NE * 2 * D), BF16, kind="Internal").ap()

        zero = W[:, 20 * 512:22 * 512]

        pieces = [HT[:, i * 512:(i + 1) * 512] for i in range(20)] + [W[:, i * 512:(i + 1) * 512] for i in range(24)]
        pieces = [a.rearrange("p (h q) -> p h q", h=H) for a in pieces]
        names = ("kc qc vc decay eg aT attnT qd kbg kdec vb b0 b1 prod tT t u wT vnew state").split()
        dn = [{n: pieces[2 * i + r] for i, n in enumerate(names)} for r in range(DIRS)]
        gst = sb("gst", [P, DIRS, H])
        bst = sb("bst", [P, DIRS, H])
        gs = sb("gs", [P, DIRS, 12])
        ge = sb("ge", [P, DIRS, 12])
        bg = sb("bg", [P, DIRS, H])

        ps = es.enter_context(nc.psum_tensor("ps", [P, 8, 512], F32))

        s_small = sem("small_inputs_loaded")
        s_w = [sem(f"weight_slot_loaded{i}") for i in range(3)]
        s_wfree = sem("weight_chunks_used")
        s_x = [sem(f"x_loaded{i}") for i in range(4)]
        s_const = sem("masks_built")
        s_pool = sem("pool_order")
        s_act = sem("act_order")
        s_dve = sem("dve_order")
        s_colT = sem("columns_transposed")
        s_col = sem("columns_ready")
        s_cs = sem("silu_c_ready")
        s_ada = sem("ada_rows_done")
        s_adar = sem("ada_rows_copied")
        s_adaT = sem("ada_columns_done")
        s_mod = sem("modulation_ready")
        s_modA = sem("scale_ready")
        s_ssq = sem("x_squares_summed")
        s_xn = sem("x_normed")
        s_xT = sem("x_transposed")
        s_hA = sem("h_left_by_act")
        s_hV = sem("h_left_by_dve")
        s_pj = sem("projection_group_done")
        s_pjf = sem("projection_bank_free")
        s_vg = sem("v_gelu_ready")
        s_vn = sem("v_normed")
        s_var = sem("v_variance_ready")
        s_lrs = sem("v_scale_ready")
        s_rt = sem("head_norm_roots")
        s_sg = sem("sgu_products_done")
        s_sgf = sem("sgu_gated")
        s_cin = sem("conv_in_ready")
        s_cout = sem("conv_done")
        s_qkv = sem("qkv_ready")
        s_sq = sem("squares_ready")
        s_ss = sem("head_norms_summed")
        s_nrm = sem("qk_normed")
        s_dbg = sem("dbg")
        s_g = sem("decays_ready")
        s_idle = sem("unread")
        e_st = Event(sem("chunk_staged"), 2)
        e_G = Event(sem("decay_sums_done"), 2)
        e_E = Event(sem("decay_differences_ready"), 2)
        e_D = Event(sem("decay_exponentials_ready"), 2)
        e_K = Event(sem("kk_products_done"), 2)
        e_A = Event(sem("a_ready"), 2)
        e_Q = Event(sem("qk_and_transposes_done"), 2)
        e_KV = Event(sem("keys_values_ready"), 2)
        e_B = Event(sem("level_blocks_ready"), 2 * LEVELS)
        e_qd = Event(sem("decayed_queries_ready"), 2)
        NL = LEVELS - 1
        e_P = Event(sem("level_first_product_done"), 2 * NL)
        e_Pc = Event(sem("level_first_product_copied"), 2 * NL)
        e_TP = Event(sem("level_second_product_done"), 2 * NL)
        e_T = Event(sem("inverse_transpose_ready"), 2 * LEVELS)
        e_X = Event(sem("inverse_turned"), 2 * NL)
        e_Xc = Event(sem("inverse_ready"), 2 * NL)
        e_u = Event(sem("u_and_w_done"), 2)
        e_uc = Event(sem("u_and_w_copied"), 2)
        e_ws = Event(sem("w_state_product_done"), 2)
        e_vn = Event(sem("new_values_ready"), 2)
        e_o = Event(sem("output_and_update_done"), 2)
        e_S = Event(sem("state_ready"), 2)
        s_ogate = sem("deltanet_done")
        s_zero = sem("zeros_ready")
        s_fill = sem("unused_rows_zeroed")
        s_wo = [sem(f"w_out_loaded{i}") for i in range(2)]
        s_xr = [sem(f"x_again_loaded{i}") for i in range(2)]
        s_rw = sem("router_inputs_loaded")
        s_g1 = sem("gate_row_done")
        s_g1c = sem("gate_row_copied")
        s_os = sem("o_roots_ready")
        s_on = sem("o_gated")
        s_oT = sem("o_transposed")
        s_mx = sem("mix_ready")
        s_y = sem("out_product_done")
        s_yr = sem("y_roots_ready")
        s_x1 = sem("x1_ready")
        s_x1r = sem("x1_roots_ready")
        s_n2 = sem("xn2_ready")
        s_x1s = [sem(f"x1_stored{i}") for i in range(2)]
        s_n2s = [sem(f"xn2_stored{i}") for i in range(2)]
        s_n2T = sem("xn2_transposed")
        s_h2A = sem("h2_left_by_act")
        s_h2V = sem("h2_left_by_dve")
        s_rt2 = sem("router_product_done")
        s_lg = sem("router_read")
        s_ch = sem("choices_ready")
        s_cnt = sem("counts_done")
        s_nb = sem("block_counts_ready")
        s_cum = sem("block_sums_done")
        s_past = sem("past_blocks_ready")
        s_exp = sem("block_experts_done")
        s_meta = sem("meta_ready")
        s_rank = sem("ranks_done")
        s_hot = sem("slot_one_hots_ready")
        s_hotu = sem("slot_one_hots_used")
        s_slot = sem("slots_ready")
        s_dve2 = sem("dve_order_at_the_end")
        s_sm = sem("gate_exponentials_ready")
        s_b3 = sem("bias_parts_loaded")
        s_b3s = sem("bias_parts_stored")
        s_b3p = sem("bias_parts_ready")
        s_bdn = sem("b_down_loaded")
        e_w = [Event(sem(f"expert_weights{j}"), 16) for j in range(6)]
        e_b3 = Event(sem("block_bias_loaded"), 16)
        e_idx = Event(sem("block_rows_named"), 1)
        e_xg = Event(sem("block_rows_gathered"), 16)
        e_xgT = Event(sem("block_rows_transposed"), 1)
        e_xa = Event(sem("xT_left_by_act"), 1)
        e_xv = Event(sem("xT_left_by_dve"), 1)
        e_gu = Event(sem("gate_up_done"), 4)
        e_g = Event(sem("gate_clamped"), 4)
        e_sg = Event(sem("gate_sigmoid_ready"), 4)
        e_act = Event(sem("activation_ready"), 4)
        e_aT = Event(sem("activation_transposed"), 4)
        e_aTc = Event(sem("activation_transposes_copied"), 4)
        e_dn = Event(sem("down_done"), 2)
        e_yc = Event(sem("block_output_copied"), 2)
        e_ys = Event(sem("block_output_stored"), 16)
        s_g2 = sem("last_gate_row_done")
        s_g2c = sem("last_gate_row_copied")
        s_mixe = sem("expert_gates_ready")
        s_gT = sem("expert_gates_transposed")
        s_gTc = sem("expert_gates_copied")
        s_bd = sem("b_down_mixed")
        s_yg = [sem(f"outputs_gathered{i}") for i in range(2)]
        s_x1l = [sem(f"x1_loaded{i}") for i in range(2)]
        s_acc = sem("experts_summed")
        s_accr = sem("expert_sum_roots_ready")
        s_fin = sem("result_ready")
        s_out = [sem(f"result_stored{i}") for i in range(2)]

        def chunk_of(s, r, out):
            if r == 0:
                return s
            return s * -1 + (NC + NA - 1 if out else NC - 1)

        def deltanet(eng, turn):
            with eng.Fori(0, NC) as s:
                turn(s, False)
            with eng.Fori(NC, NA) as s:
                turn(s, True)

        def spread(cols4):
            return cols4.unsqueeze(2).to_broadcast([P, H, P])

        def bank(r, i):
            return ps[:, 4 * r + i, :].rearrange("p (h q) -> p h q", h=H)

        block = es.enter_context(nc.Block())

        def rowvec(ap, n=P):
            return ap.partition_broadcast(n)

        stream = [w_ada[0, :, i * 512:(i + 1) * 512] for i in range(NADA)]
        stream += [w_in[0, :, o:o + 512] for o in (U0, V0, Z0, 0, 512, 1024)]
        NSTR = len(stream)

        def chunk(q):
            return slot(q % 3).rearrange("p (k n) -> p k n", k=KD)

        SPANS = [(CTX, 512), (CTX + 512, 512), (0, CTX)]
        G_U, G_V, G_Z, G_QKV = 1, 9, 17, 25
        NG = G_QKV + 3 * 3 * H

        def store_x1(sp, n):
            sp.wait_ge(s_x1, n + 1)
            sp.dma_start(x1_d[n * P:(n + 1) * P, :], x1[:, n % 2, :]).then_inc(s_x1s[n % 2], 16)
            sp.wait_ge(s_n2, n + 1)
            sp.dma_start(xn_d[n * P:(n + 1) * P, :], xn2[:, n % 2, :]).then_inc(s_n2s[n % 2], 16)

        @block.sync
        def _(sp):
            for e in [*e_w, e_b3]:
                e.ahead(sp)
            sp.dma_start(rows[0:48, 0, :], b_ada.rearrange("a (r q) -> (a r) q", q=P)).then_inc(s_small, 16)
            sp.dma_start(rows[48:80, 0, :], norm_g.rearrange("a f (r q) -> (a f r) q", q=P)).then_inc(s_small, 16)
            sp.dma_start(rows[80:88, 0, :], c.rearrange("a (r q) -> (a r) q", q=P)).then_inc(s_small, 16)
            sp.dma_start(rows[88:96, 0, :], c_ctx.rearrange("(r q) -> r q", q=P)).then_inc(s_small, 16)
            sp.dma_start(rows[0:36, 1, :], conv_w.rearrange("a j (r q) -> (a j r) q", q=P)).then_inc(s_small, 16)
            for q in range(NSTR):
                if q >= 3:
                    sp.wait_ge(s_wfree, q - 2)
                sp.dma_start(chunk(q), stream[q].rearrange("(k p) n -> p k n", p=P)).then_inc(s_w[q % 3], 16)
            sp.wait_ge(s_zero, 1)
            first = SEQ * TOPK // P
            sp.dma_start(y_d[first * P:, :].rearrange("(b p) d -> p b d", p=P),
                         zero.unsqueeze(1).to_broadcast([P, 64 - first, D])).then_inc(s_fill, 16)
            sp.wait_ge(s_fill, 16)
            sp.wait_ge(s_ogate, 1)
            for i in range(2):
                sp.dma_start(wo[i], w_out[0, :, i * 512:(i + 1) * 512].rearrange("(k p) n -> p k n", p=P)).then_inc(s_wo[i], 16)
            sp.dma_start(rw, router_w[0].rearrange("(k p) e -> p k e", p=P)).then_inc(s_rw, 16)
            sp.dma_start(rb, rowvec(router_b[0])).then_inc(s_rw, 16)
            sp.dma_start(b_raw, b_gu[0].rearrange("e (q c) -> (e q) c", c=512)).then_inc(s_b3, 16)
            for n in range(NT):
                if n >= 2:
                    sp.wait_ge(s_x1, n - 1)
                sp.dma_start(xr[:, n % 2, :], x[0, n * P:(n + 1) * P, :]).then_inc(s_xr[n % 2], 16)
                if n >= 1:
                    store_x1(sp, n - 1)
            store_x1(sp, NT - 1)
            sp.wait_ge(s_b3p, 1)
            sp.dma_start(b3_d.rearrange("j (p c) -> p j c", p=P), b_part).then_inc(s_b3s, 16)
            sp.dma_start(bdn[0:NE, :], b_down[0]).then_inc(s_bdn, 16)
            sp.wait_ge(s_b3s, 16)

            sp.wait_ge(s_meta, 1)
            nblk = sp.value_load(meta[0:1, 128:129], min_val=SEQ * TOPK // P, max_val=MAXB)
            with sp.Fori(0, MAXB) as t:
                with sp.If(t < nblk):
                    e = sp.value_load(meta[0:1, bass.ds(t, 1)], min_val=0, max_val=NE - 1)
                    new = sp.value_load(meta[0:1, bass.ds(t + 64, 1)], min_val=0, max_val=1)
                    for j in range(6):
                        e_gu.before(sp, t, j) if j < 4 else e_dn.before(sp, t, j - 4)
                        src = w_gu[0, bass.ds(e, 1), :, j * 512:(j + 1) * 512] if j < 4 else \
                            w_down[0, bass.ds(e, 1), :, (j - 4) * 512:(j - 3) * 512]
                        sp.dma_start(slot(j).rearrange("p (k n) -> p k n", k=KD),
                                     src.rearrange("a (k p) n -> p (a k) n", p=P), cond=new > 0).then_inc(e_w[j].sem, 16)
                        if j == 3:
                            sp.dma_start(bias3[0:3, :], b3_d[:, bass.ds(e * 2 * D, 2 * D)]).then_inc(e_b3.sem, 16)
            if dbg is not None:
                sp.wait_ge(s_hotu, 32)
                sp.dma_start(dbg, HT[:]).then_inc(s_dbg, 16)
                sp.wait_ge(s_dbg, 16)

        @block.gpsimd
        def _(pool):
            link = Link(pool, s_pool)
            link(pool.memset(ident[:], 0.0))
            link(pool.memset(ones[:], 1.0))
            link(pool.memset(eps_c[:], EPS))
            link(pool.memset(mhalf[:], -0.5))
            link(pool.memset(zmask[:], 0.0))
            link(pool.affine_select(out=ident[:], in_=ident[:], compare_op=ALU.not_equal, fill=1.0,
                                    base=0, pattern=[[-1, P]], channel_multiplier=1))
            for r in range(DIRS):
                s = 1 - 2 * r
                link(pool.affine_select(out=tri[:, r, :], in_=ones[:], compare_op=ALU.is_ge, fill=0.0,
                                        base=0, pattern=[[s, P]], channel_multiplier=-s))
                link(pool.affine_select(out=zmask[:, r, :], in_=zmask[:, r, :], compare_op=ALU.is_ge,
                                        fill=-HUGE, base=0, pattern=[[s, P]], channel_multiplier=-s))
            link(pool.iota(idx_i[:, 0:1], pattern=[[0, 1]], base=0, channel_multiplier=1))
            for l in range(1, LEVELS):
                link(pool.iota(same[:, l - 1, :], pattern=[[1, P >> l], [0, 1 << l]], base=0,
                               channel_multiplier=0, allow_small_or_imprecise_dtypes=True))
            link(pool.iota(iota[:], pattern=[[1, P]], base=0, channel_multiplier=0,
                           allow_small_or_imprecise_dtypes=True))
            link(pool.iota(tokid[:], pattern=[[P, NT]], base=0, channel_multiplier=1,
                           allow_small_or_imprecise_dtypes=True))
            pool.iota(idx_f[:, 0:1], pattern=[[0, 1]], base=0, channel_multiplier=0,
                      allow_small_or_imprecise_dtypes=True).then_inc(s_const, 1)
            pool.dma_start(wba[:], w_in[0, :, QKV:QKV + BA].rearrange("(k p) n -> p k n", p=P)).then_inc(s_x[3], 16)
            for n in range(NT):
                pool.wait_ge(s_var, n + 1)
                link(pool.tensor_scalar(lrs[:], mv[:, :, 1], EPS, None, ALU.add))
                pool.tensor_tensor(lrs[:], lrs[:], mhalf[:, 0:H], ALU.pow).then_inc(s_lrs, 1)

            pool.wait_ge(s_g, 1)
            e_st.ahead(pool)
            e_B.ahead(pool)
            e_qd.ahead(pool)

            def turn(s, out):
                for r in range(DIRS):
                    d, n = dn[r], chunk_of(s, r, out)
                    e_Q.before(pool, s, r)
                    e_KV.before(pool, s, r)
                    pool.sem_inc(s_idle, 1)
                    e_qd.before(pool, s, r)
                    pool.sem_inc(s_idle, 1)
                    pool.tensor_copy(gst[:, r, :], gdec[:, bass.ds(n, 1), 4 * r:4 * r + 4].rearrange("p a h -> p (a h)"))
                    pool.tensor_copy(bst[:, r, :], beta[:, bass.ds(n, 1), 4 * r:4 * r + 4].rearrange("p a h -> p (a h)"))
                    pool.tensor_copy(d["kc"], qkvT[:, H:2 * H, bass.ds(n * P, P)])
                    if out:
                        pool.tensor_copy(d["qc"], qkvT[:, 0:H, bass.ds(n * P, P)])
                    pool.tensor_copy(d["vc"], qkvT[:, 2 * H:3 * H, bass.ds(n * P, P)]).then_inc(e_st.sem, 1)
                for l in range(LEVELS):
                    for r in range(DIRS):
                        d = dn[r]
                        if l == 0:
                            e_A.now(pool, s, r)
                            pool.sem_inc(s_idle, 1)
                        if l >= 3:
                            e_P.now(pool, s, 2 * (l - 3) + r)
                            pool.sem_inc(s_idle, 1)
                        elif l >= 1:
                            e_P.before(pool, s, 2 * (l + LEVELS - 4) + r)
                            pool.sem_inc(s_idle, 1)
                        mask = neg0 if l == 0 else same[:, l - 1, :]
                        dst = d["u"] if l == 0 else d["b%d" % (l % 2)]
                        if l == 0:
                            e_vn.before(pool, s, r)
                            pool.sem_inc(s_idle, 1)
                        m = mask[:] if l == 0 else mask
                        pool.tensor_tensor(dst, d["aT"], m.unsqueeze(1).to_broadcast([P, H, P]),
                                           ALU.mult).then_inc(e_B.sem, 1)
                        if l == 1 and out:
                            e_D.now(pool, s, r)
                            pool.sem_inc(s_idle, 1)
                            e_o.before(pool, s, r)
                            pool.sem_inc(s_idle, 1)
                            pool.tensor_tensor(d["qd"], d["qc"], d["eg"], ALU.mult).then_inc(e_qd.sem, 1)
                        elif l == 1:
                            pool.sem_inc(e_qd.sem, 1)

            deltanet(pool, turn)

            pool.wait_ge(s_b3, 16)
            for j in range(3):
                link(pool.tensor_copy(b_part[:, j, :], b_raw))
                if j < 2:
                    link(pool.tensor_tensor(b_raw, b_raw, b_part[:, j, :], ALU.subtract))
            pool.sem_inc(s_b3p, 1)

            for i in range(2):
                pool.wait_ge(s_n2s[i], 16 * NT // 2)
            pool.wait_ge(s_slot, 1)
            e_idx.ahead(pool)

            nblk = pool.value_load(meta[0:1, 128:129], min_val=SEQ * TOPK // P, max_val=MAXB)
            link(pool.tensor_copy(idx[:], slots[:, 0:1]))
            pool.indirect_dma_start(out=xg, out_offset=None, in_=xn_d,
                                    in_offset=bass.IndirectOffsetOnAxis(ap=idx[:, 0:1], axis=0),
                                    bounds_check=SEQ - 1).then_inc(e_xg.sem, 16)
            with pool.Fori(0, MAXB) as t:
                with pool.If(t < nblk):
                    pool.wait_ge(e_xg.sem, 16 * t + 16)
                    pool.sem_inc(s_idle, 1)
                    pool.tensor_copy(idx[:], slots[:, bass.ds(t + 1, 1)]).then_inc(e_idx.sem, 1)
                    pool.wait_ge(e_idx.sem, t + 2)
                    pool.sem_inc(s_idle, 1)
                    e_xgT.now(pool, t, 0)
                    pool.sem_inc(s_idle, 1)
                    pool.indirect_dma_start(out=xg, out_offset=None, in_=xn_d,
                                            in_offset=bass.IndirectOffsetOnAxis(ap=idx[:, 0:1], axis=0),
                                            bounds_check=SEQ - 1).then_inc(e_xg.sem, 16)
            pool.wait_ge(e_ys.sem, nblk * 16 + 16)
            pool.sem_inc(s_idle, 1)
            for n in range(NT):
                if n >= 2:
                    pool.wait_ge(s_acc, n - 1)
                for k in range(TOPK):
                    pool.indirect_dma_start(out=yg[:, n % 2, k, :], out_offset=None, in_=y_d,
                                            in_offset=bass.IndirectOffsetOnAxis(ap=dest_i[:, n * TOPK + k:n * TOPK + k + 1].bitcast(U32), axis=0),
                                            bounds_check=64 * P - 1).then_inc(s_yg[n % 2], 16)

        def meta_wait(eng):
            eng.wait_ge(s_meta, 1)
            return meta[0:1, 128:129]

        @block.scalar
        def _(act):
            link = Link(act, s_act)

            def load_x(i):
                src = ctx_in[0, i * P:(i + 1) * P, :] if i < NC else x[0, (i - NC) * P:(i - NC + 1) * P, :]
                act.dma_start(xs[:, i % 2, :], src).then_inc(s_x[i % 2], 16)

            load_x(0)
            load_x(1)
            for dst, src in ((sgu_bb, sgu_b.rearrange("a g q -> (a g q)")),
                             (ln_gb, sgu_ln_g.rearrange("a g q -> (a g q)")),
                             (ln_bb, sgu_ln_b.rearrange("a g q -> (a g q)")),
                             (alog[:], a_log.rearrange("a r h -> (a r h)")),
                             (dtb[:], dt_bias.rearrange("a r h -> (a r h)")),
                             (gng[:], gdn_norm_g.rearrange("a q -> (a q)"))):
                act.dma_start(dst, rowvec(src)).then_inc(s_x[2], 16)
            act.dma_start(sgu_raw, sgu_w[0].rearrange("g p q -> p g q")).then_inc(s_x[2], 16)

            act.wait_ge(s_colT, 1)
            link(act.activation(cols[:], ps[:, 0, 0:96], ACT.Copy))
            link(act.activation(ccol[:], ps[:, 1, 0:36], ACT.Copy))
            link(act.activation(sguT, ps[:, 2, :].rearrange("p (g q) -> p g q", g=H), ACT.Copy))
            for s in range(2):
                last = act.activation(cs[:, :, s], cols[:, 80 + 8 * s:88 + 8 * s], ACT.Silu)
                link(last)
            act.sem_inc(s_cs, 1)
            for q in range(NADA):
                act.wait_ge(s_ada, q + 1)
                if q >= 2:
                    act.wait_ge(s_adaT, q - 1)
                act.activation(modrow[0:2, q % 2, :], ps[0:2, q % 2, :], ACT.Copy).then_inc(s_adar, 1)
            for i in range(NA):
                act.wait_ge(s_x[i % 2], 16 * (i // 2 + 1))
                link(act.activation(junk, xs[:, i % 2, :], ACT.Square, accum_out=ssq[:, i:i + 1]))
                act.activation(rst[:, i:i + 1], ssq[:, i:i + 1], ACT.Sqrt, scale=1.0 / D,
                               bias=eps_c[:, 0:1]).then_inc(s_ssq, 1)
                act.wait_ge(s_xT, i + 1)
                if i + 2 < NA:
                    load_x(i + 2)
                s = 1 if i < NC else 0
                t0 = i * P
                for k in range(4, KD):
                    last = act.activation(hT[:, k, t0:t0 + P], ps[:, 2 * (i % 2) + 1, (k - 4) * P:(k - 3) * P],
                                          ACT.Identity, scale=scA[:, s, k:k + 1], bias=modc[:, k, s:s + 1])
                last.then_inc(s_hA, 1)

            def take(g):
                act.wait_ge(s_pj, g + 1)

            take(0)
            act.activation(ba[:], ps[:, 0, 0:NA * BA].rearrange("p (n b) -> p n b", n=NA), ACT.Copy).then_inc(s_pjf, 1)
            for g in range(G_U, G_V):
                take(g)
                ct, half = (g - G_U) // 2, (g - G_U) % 2
                act.activation(uT[:, ct, half * 512:(half + 1) * 512], ps[:, g % 6, :],
                               ACT.Gelu_apprx_tanh).then_inc(s_pjf, 1)
            for g in range(G_V, G_Z):
                take(g)
                n = g - G_V
                if n >= 2:
                    act.wait_ge(s_vn, n - 1)
                link(act.activation(v_gelu[:, n % 2, :], ps[:, g % 6, :], ACT.Gelu_apprx_tanh))
                act.sem_inc(s_vg, 1)
                act.sem_inc(s_pjf, 1)
            for g in range(G_Z, G_QKV):
                take(g)
                act.activation(zs[:, g - G_Z, :], ps[:, g % 6, :], ACT.Silu).then_inc(s_pjf, 1)

            def silu(m):
                ct, (t0, n) = m // 3, SPANS[m % 3]
                act.wait_ge(s_cout, m + 1)
                act.activation(qkvT[:, ct, t0:t0 + n], conv_out[:, m % 2, 0:n], ACT.Silu).then_inc(s_qkv, 1)

            for m in range(NG - G_QKV):
                g = G_QKV + m
                n = SPANS[m % 3][1]
                take(g)
                if m >= 2:
                    act.wait_ge(s_cout, m - 1)
                link(act.activation(conv_in[:, m % 2, 0:n], ps[:, g % 6, 0:n], ACT.Copy))
                act.sem_inc(s_cin, 1)
                act.sem_inc(s_pjf, 1)
                if m >= 1:
                    silu(m - 1)
            silu(NG - G_QKV - 1)
            def root(m):
                n = SPANS[m % 3][1]
                act.wait_ge(s_ss, m + 1)
                if m >= 2:
                    act.wait_ge(s_nrm, m - 1)
                act.activation(conv_out[:, m % 2, 0:n], ps[:, m % 2, 0:n], ACT.Sqrt, bias=eps_c[:, 0:1]).then_inc(s_rt, 1)

            for m in range(24):
                ct, (t0, n) = m // 3, SPANS[m % 3]
                act.wait_ge(s_qkv, m + 1)
                if m >= 2:
                    act.wait_ge(s_ss, m - 1)
                act.activation(conv_in[:, m % 2, 0:n], qkvT[:, ct, t0:t0 + n], ACT.Square).then_inc(s_sq, 1)
                if m >= 1:
                    root(m - 1)
            root(23)
            act.wait_ge(s_modA, 3)
            act.activation(beta[:], ba[:, :, 0:8], ACT.Sigmoid)
            link(act.activation(batmp[:], gdec[:], ACT.Abs))
            link(act.activation(batmp[:], batmp[:], ACT.Exp, scale=-1.0))
            link(act.activation(alog[:], alog[:], ACT.Exp))
            link(act.activation(batmp[:], batmp[:], ACT.Ln, bias=1.0))
            act.sem_inc(s_modA, 1)

            for e in (e_D, e_Pc, e_Xc, e_uc):
                e.ahead(act)

            def turn(s, out):
                for r in range(DIRS):
                    d = dn[r]
                    e_E.now(act, s, r)
                    e_A.before(act, s, r)
                    if out:
                        e_qd.before(act, s, r)
                        act.activation(d["eg"], bank(r, 0), ACT.Exp)
                    act.activation(ge[:, r, :], gs[:, r, :], ACT.Exp)
                    act.activation(d["decay"], d["decay"], ACT.Exp).then_inc(e_D.sem, 1)
                for l in range(LEVELS):
                    for r in range(DIRS):
                        d = dn[r]
                        if l >= 1:
                            e_P.now(act, s, 2 * (l - 1) + r)
                            act.activation(d["prod"], bank(r, 0), ACT.Copy).then_inc(e_Pc.sem, 1)
                    for r in range(DIRS):
                        d = dn[r]
                        if l < NL:
                            e_X.now(act, s, 2 * l + r)
                            act.activation(d["t"], bank(r, 2), ACT.Copy).then_inc(e_Xc.sem, 1)
                for r in range(DIRS):
                    d = dn[r]
                    e_u.now(act, s, r)
                    act.activation(d["wT"], bank(r, 1), ACT.Copy)
                    act.activation(d["u"], bank(r, 0), ACT.Copy).then_inc(e_uc.sem, 1)

            deltanet(act, turn)

            act.wait_ge(s_ogate, 1)
            act.wait_ge(s_g1, 1)
            act.activation(g1row, ps[:, 6:8, :].rearrange("p b c -> p (b c)"), ACT.Copy).then_inc(s_g1c, 1)

            def o_roots(n):
                for h in range(H):
                    last = act.activation(junk2[:, 0:P], o_acc[:, n, h * P:(h + 1) * P], ACT.Square,
                                          accum_out=ssq[:, h:h + 1])
                    link(last)
                if n >= 1:
                    act.wait_ge(s_on, n)
                act.activation(rst[:, 0:H], ssq[:, 0:H], ACT.Sqrt, scale=1.0 / P, bias=eps_c[:, 0:1]).then_inc(s_os, 1)
                act.wait_ge(s_os, n + 1)

            o_roots(0)
            for n in range(NT):
                if n + 1 < NT:
                    o_roots(n + 1)
                act.wait_ge(s_oT, n + 1)
                act.activation(mixT[:, n % 2], ps[:, n % 2, :].rearrange("p (k t) -> p k t", k=H), ACT.Copy).then_inc(s_mx, 1)
                act.wait_ge(s_y, n + 1)
                link(act.activation(junk2, ps[:, 2:4, :].rearrange("p b c -> p (b c)"), ACT.Square,
                                    accum_out=ssq[:, 8:9]))
                act.activation(rst[:, 8:9], ssq[:, 8:9], ACT.Sqrt, scale=1.0 / D, bias=eps_c[:, 0:1]).then_inc(s_yr, 1)
                act.wait_ge(s_yr, n + 1)
                act.wait_ge(s_x1, n + 1)
                link(act.activation(junk2, x1[:, n % 2, :], ACT.Square, accum_out=ssq[:, 9:10]))
                act.activation(rst[:, 9:10], ssq[:, 9:10], ACT.Sqrt, scale=1.0 / D, bias=eps_c[:, 0:1]).then_inc(s_x1r, 1)
                act.wait_ge(s_x1r, n + 1)
                act.wait_ge(s_n2T, n + 1)
                if n >= 2:
                    act.wait_ge(s_rt2, n - 1)
                for k in range(4, KD):
                    last = act.activation(h2T[:, n % 2, k, :], ps[:, 5, (k - 4) * P:(k - 3) * P], ACT.Identity,
                                          scale=sc2[:, k:k + 1], bias=modc[:, 24 + k, 0:1])
                last.then_inc(s_h2A, 1)
            act.wait_ge(s_ch, NT)
            act.wait_ge(s_sm, 1)
            act.activation(gates, gates, ACT.Exp).then_inc(s_sm, 1)

            nblk = act.value_load(meta_wait(act), min_val=SEQ * TOPK // P, max_val=MAXB)
            for e in (e_xa, e_sg, e_aTc, e_yc, e_ys):
                e.ahead(act)

            def xT_half():
                for k in range(4, KD):
                    last = act.activation(xT[:, k, :], ps[:, 1, (k - 4) * P:(k - 3) * P], ACT.Identity,
                                          scale=sc2[:, k:k + 1], bias=modc[:, 24 + k, 0:1])
                last.then_inc(e_xa.sem, 1)

            act.wait_ge(e_xgT.sem, 2)
            xT_half()
            with act.Fori(0, MAXB) as t:
                with act.If(t < nblk):
                    def sigmoid(j):
                        e_g.now(act, t, j)
                        act.activation(sig_n[:, j % 2, :], gate_n[:, j % 2, :], ACT.Sigmoid, scale=ALPHA).then_inc(e_sg.sem, 1)

                    def copy_T(j):
                        e_aT.now(act, t, j)
                        if j == 0:
                            e_dn.before(act, t, 1)
                        act.activation(actT[:, 2 * j:2 * j + 2, :],
                                       ps[:, 4 + 3 * (j % 2), 0:256].rearrange("p (k t) -> p k t", k=2),
                                       ACT.Copy).then_inc(e_aTc.sem, 1)

                    sigmoid(0)
                    for j in range(1, 4):
                        sigmoid(j)
                        copy_T(j - 1)
                    act.wait_ge(e_xgT.sem, t + 3)
                    xT_half()
                    copy_T(3)
                    for i in range(2):
                        e_dn.now(act, t, i)
                        if i == 0:
                            e_ys.before(act, t, 15)
                        act.activation(ysb[:, i * 512:(i + 1) * 512], ps[:, 5 + i, :], ACT.Copy).then_inc(e_yc.sem, 1)
                    e_yc.now(act, t, 1)
                    act.dma_start(y_d[bass.ds(t * P, P), :], ysb).then_inc(e_ys.sem, 16)

            act.wait_ge(s_g2, 1)
            act.activation(g2row, ps[:, 0:2, :].rearrange("p b c -> p (b c)"), ACT.Copy).then_inc(s_g2c, 1)

            def x1_load(n):
                if n >= 2:
                    act.wait_ge(s_fin, n - 1)
                act.dma_start(x1r[:, n % 2, :], x1_d[n * P:(n + 1) * P, :]).then_inc(s_x1l[n % 2], 16)

            for i in range(2):
                act.wait_ge(s_x1s[i], 16 * NT // 2)
                x1_load(i)
            for n in range(NT):
                act.wait_ge(s_gT, n + 1)
                act.activation(gT[0:NE, :], ps[0:NE, 2, 0:P], ACT.Copy).then_inc(s_gTc, 1)
                act.wait_ge(s_acc, n + 1)
                link(act.activation(junk3, acc, ACT.Square, accum_out=ssq[:, 0:1]))
                act.activation(rst[:, 0:1], ssq[:, 0:1], ACT.Sqrt, scale=1.0 / D, bias=eps_c[:, 0:1]).then_inc(s_accr, 1)
                act.wait_ge(s_accr, n + 1)
                act.wait_ge(s_fin, n + 1)
                act.dma_start(out[0, n * P:(n + 1) * P, :], x1r[:, n % 2, :]).then_inc(s_out[n % 2], 16)
                if n + 2 < NT:
                    act.wait_ge(s_out[n % 2], 16 * (n // 2 + 1))
                    x1_load(n + 2)
            for i in range(2):
                act.wait_ge(s_out[i], 16 * NT // 2)

        @block.vector
        def _(dve):
            link = Link(dve, s_dve)
            dve.wait_ge(s_const, 1)
            for l in range(1, LEVELS):
                link(dve.tensor_single_scalar(idx_i[:, l:l + 1], idx_i[:, 0:1], l, ALU.logical_shift_right))
            link(dve.tensor_copy(idx_f[:, 1:7], idx_i[:, 1:7]))
            for l in range(1, LEVELS):
                link(dve.tensor_scalar(same[:, l - 1, :], same[:, l - 1, :], idx_f[:, l:l + 1], None, ALU.is_equal))
            link(dve.tensor_tensor(neg0[:], ident[:], same[:, 0, :], ALU.subtract))
            for l in range(1, LEVELS - 1):
                link(dve.tensor_tensor(same[:, l - 1, :], same[:, l - 1, :], same[:, l, :], ALU.subtract))
            link(dve.tensor_tensor(same[:, LEVELS - 2, :], same[:, LEVELS - 2, :], ones[:], ALU.subtract))
            dve.wait_ge(s_act, 1)
            for q in range(NADA):
                dve.wait_ge(s_adaT, q + 1)
                link(dve.tensor_tensor(modc[:, 4 * q:4 * q + 4, :],
                                       ps[:, 2 + q % 2, 0:8].rearrange("p (a s) -> p a s", s=2),
                                       cols[:, 4 * q:4 * q + 4].unsqueeze(2).to_broadcast([P, 4, 2]), ALU.add))
                dve.sem_inc(s_mod, 1)
            for s in range(2):
                link(dve.scalar_tensor_tensor(scA[:, s, :], modc[:, 8:16, s], 1.0, cols[:, 48:56], ALU.add, ALU.mult))
            link(dve.scalar_tensor_tensor(sc2[:], modc[:, 32:40, 0], 1.0, cols[:, 64:72], ALU.add, ALU.mult))
            link(dve.tensor_tensor(gvec[:, 0, :], modc[:, 16:24, 0], cols[:, 56:64], ALU.mult))
            link(dve.tensor_tensor(gvec[:, 1, :], modc[:, 40:48, 0], cols[:, 72:80], ALU.mult))
            dve.sem_inc(s_modA, 1)
            for i in range(NA):
                dve.wait_ge(s_ssq, i + 1)
                link(dve.reciprocal(rst[:, i:i + 1], rst[:, i:i + 1]))
                if i >= 2:
                    dve.wait_ge(s_xT, i - 1)
                link(dve.tensor_scalar(xs[:, 2 + i % 2, :], xs[:, i % 2, :], rst[:, i:i + 1], None, ALU.mult))
                dve.sem_inc(s_xn, 1)
                dve.wait_ge(s_xT, i + 1)
                s, t0 = (1 if i < NC else 0), i * P
                for k in range(4):
                    last = dve.tensor_scalar(hT[:, k, t0:t0 + P], ps[:, 2 * (i % 2), k * P:(k + 1) * P],
                                             scA[:, s, k:k + 1], modc[:, k, s:s + 1], ALU.mult, ALU.add)
                last.then_inc(s_hV, 1)
            dve.wait_ge(s_pjf, 1)
            dve.wait_ge(s_x[2], 16 * 7)
            link(dve.tensor_tensor(gdec[:], ba[:, :, 8:16], dtb[:].unsqueeze(1).to_broadcast([P, NA, 8]), ALU.add))
            dve.sem_inc(s_modA, 2)
            def gate(n):
                dve.wait_ge(s_sg, n + 1)
                tmp = v_norm[:, n % 2, :]
                link(dve.tensor_tensor(tmp, ps[:, 6 + n % 2, :], sgu_bb, ALU.add))
                u = uT[:, :, n * P:(n + 1) * P]
                dve.tensor_tensor(u, u, tmp.rearrange("p (g q) -> p g q", g=H), ALU.mult).then_inc(s_sgf, 1)

            for n in range(NT):
                dve.wait_ge(s_vg, n + 1)
                v = v_gelu[:, n % 2, :]
                for g in range(H):
                    last = dve.bn_stats(stat[:, g, :], v[:, g * P:(g + 1) * P])
                link(last)
                for g in range(H):
                    last = dve.bn_aggr(mv[:, g, :], stat[:, g, :])
                link(last)
                dve.sem_inc(s_var, 1)
                dve.wait_ge(s_lrs, n + 1)
                for g in range(H):
                    last = dve.tensor_scalar(v[:, g * P:(g + 1) * P], v[:, g * P:(g + 1) * P], mv[:, g, 0:1],
                                             lrs[:, g:g + 1], ALU.subtract, ALU.mult)
                link(last)
                link(dve.tensor_tensor(v, v, ln_gb, ALU.mult))
                if n >= 1:
                    gate(n - 1)
                if n >= 2:
                    dve.wait_ge(s_sgf, n - 1)
                link(dve.tensor_tensor(v_norm[:, n % 2, :], v, ln_bb, ALU.add))
                dve.sem_inc(s_vn, 1)
            gate(NT - 1)
            for m in range(NG - G_QKV):
                ct, n = m // 3, SPANS[m % 3][1]
                L = ROW if m % 3 < 2 else CTX
                dve.wait_ge(s_cin, m + 1)
                if m >= 2:
                    dve.wait_ge(s_qkv, m - 1)
                xi = conv_in[:, m % 2, 0:n].rearrange("p (r l) -> p r l", l=L)
                yo = conv_out[:, m % 2, 0:n].rearrange("p (r l) -> p r l", l=L)
                wc = [ccol[:, j * 12 + ct:j * 12 + ct + 1] for j in range(3)]
                link(dve.tensor_scalar(yo, xi, wc[1], None, ALU.mult))
                link(dve.scalar_tensor_tensor(yo[:, :, 1:L], xi[:, :, 0:L - 1], wc[0], yo[:, :, 1:L], ALU.mult, ALU.add))
                dve.scalar_tensor_tensor(yo[:, :, 0:L - 1], xi[:, :, 1:L], wc[2], yo[:, :, 0:L - 1],
                                         ALU.mult, ALU.add).then_inc(s_cout, 1)
            for m in range(24):
                ct, (t0, n) = m // 3, SPANS[m % 3]
                dve.wait_ge(s_rt, m + 1)
                r = conv_out[:, m % 2, 0:n]
                link(dve.reciprocal(r, r))
                t = qkvT[:, ct, t0:t0 + n]
                dve.scalar_tensor_tensor(t, t, float(P) ** -0.5 if ct < H else 1.0, r, ALU.mult,
                                         ALU.mult).then_inc(s_nrm, 1)
            dve.wait_ge(s_modA, 4)
            link(dve.tensor_scalar(gdec[:], gdec[:], 0.0, None, ALU.max))
            link(dve.tensor_tensor(gdec[:], gdec[:], batmp[:], ALU.add))
            link(dve.scalar_tensor_tensor(gdec[:], gdec[:], -1.0, alog[:].unsqueeze(1).to_broadcast([P, NA, 8]),
                                          ALU.mult, ALU.mult))
            dve.sem_inc(s_g, 1)
            link(dve.memset(slot(5), 0.0))
            link(dve.memset(zero, 0.0))
            dve.sem_inc(s_zero, 1)
            for r in range(DIRS):
                link(dve.memset(dn[r]["state"], 0.0))
            for e in (e_E, e_A, e_KV, e_T, e_vn, e_S):
                e.ahead(dve)

            def turn(s, out):
                o_at = [o_acc[:, bass.ds(chunk_of(s, r, out) - NC, 1), :].rearrange("p a (h q) -> p (a h) q", h=H)
                        if out else None for r in range(DIRS)]
                link.turn(s - NC if out else s, LINKS[out])
                for r in range(DIRS):
                    d = dn[r]
                    e_G.now(dve, s, r)
                    small = bank(r, 3)[:, 0, :]
                    e_D.before(dve, s, r)
                    link(dve.tensor_copy(gs[:, r, 0:8], small[:, 0:8]))
                    dve.tensor_tensor(gs[:, r, 8:12], gs[:, r, 4:8], gs[:, r, 0:4], ALU.subtract)
                    for h in range(H):
                        last = dve.scalar_tensor_tensor(d["decay"][:, h, :], bank(r, 0)[:, h, :], gs[:, r, h:h + 1],
                                                        zmask[:, r, :], ALU.subtract, ALU.min)
                    last.then_inc(e_E.sem, 1)
                for r in range(DIRS):
                    d = dn[r]
                    e_K.now(dve, s, r)
                    e_D.now(dve, s, r)
                    e_B.before(dve, s, 2 * NL + r)
                    link(dve.tensor_tensor(d["aT"], bank(r, 2), d["decay"], ALU.mult))
                    dve.tensor_tensor(d["aT"], d["aT"], bank(r, 1), ALU.mult).then_inc(e_A.sem, 1)
                for r in range(DIRS):
                    d = dn[r]
                    e_Q.now(dve, s, r)
                    if out:
                        dve.tensor_tensor(d["attnT"], bank(r, 3), d["decay"], ALU.mult)
                    link(dve.tensor_tensor(bg[:, r, :], bst[:, r, :], ge[:, r, 0:4], ALU.mult))
                    dve.tensor_tensor(d["kbg"], bank(r, 0), spread(bg[:, r, :]), ALU.mult)
                    dve.tensor_tensor(d["kdec"], bank(r, 0), spread(ge[:, r, 8:12]), ALU.mult)
                    dve.tensor_tensor(d["vb"], bank(r, 1), spread(bst[:, r, :]), ALU.mult).then_inc(e_KV.sem, 1)
                for l in range(LEVELS):
                    for r in range(DIRS):
                        d = dn[r]
                        if l == 0:
                            e_B.now(dve, s, r)
                            dve.tensor_tensor(d["tT"], d["u"], ident[:].unsqueeze(1).to_broadcast([P, H, P]),
                                              ALU.add).then_inc(e_T.sem, 1)
                        else:
                            e_TP.now(dve, s, 2 * (l - 1) + r)
                            dve.tensor_tensor(d["tT"], d["tT"], bank(r, 1), ALU.add).then_inc(e_T.sem, 1)
                for r in range(DIRS):
                    d = dn[r]
                    e_uc.now(dve, s, r)
                    e_ws.now(dve, s, r)
                    dve.tensor_tensor(d["vnew"], d["u"], bank(r, 2), ALU.subtract).then_inc(e_vn.sem, 1)
                for r in range(DIRS):
                    d = dn[r]
                    o = o_at[r]
                    e_o.now(dve, s, r)
                    if out:
                        link(dve.tensor_tensor(o, o, bank(r, 0), ALU.add))
                    for h in range(H):
                        last = dve.scalar_tensor_tensor(d["state"][:, h, :], d["state"][:, h, :], ge[:, r, 4 + h:5 + h],
                                                        bank(r, 3)[:, h, :], ALU.mult, ALU.add)
                    last.then_inc(e_S.sem, 1)
                link.end(NA - NC if out else NC)

            deltanet(dve, turn)
            dve.wait_ge(e_S.sem, 2 * NA + 2)
            dve.sem_inc(s_ogate, 1)

            dve.wait_ge(s_x[2], 16 * 7)
            link(dve.tensor_tensor(zs.rearrange("p n (h q) -> p (n h) q", h=H), zs.rearrange("p n (h q) -> p (n h) q", h=H),
                                   gng[:].unsqueeze(1).to_broadcast([P, NT * H, P]), ALU.mult))

            def gate_o(n):
                dve.wait_ge(s_os, n + 1)
                link(dve.reciprocal(rst[:, 4:8], rst[:, 0:H]))
                if n >= 2:
                    dve.wait_ge(s_oT, n - 1)
                for h in range(H):
                    cc = slice(h * P, (h + 1) * P)
                    last = dve.scalar_tensor_tensor(on[:, n % 2, cc], o_acc[:, n, cc], rst[:, 4 + h:5 + h],
                                                    zs[:, n, cc], ALU.mult, ALU.mult)
                last.then_inc(s_on, 1)

            def route(n):
                dve.wait_ge(s_rt2, n + 1)
                lg = base
                if n == 0:
                    dve.wait_ge(s_rw, 32)
                link(dve.tensor_tensor(lg, ps[:, 6, 0:NE], rb, ALU.add))
                dve.sem_inc(s_lg, 1)
                link(dve.max(top[:, n, :], lg))
                link(dve.max_index(top_i[:], top[:, n, :], lg))
                link(dve.tensor_copy(top_f[:], top_i[:]))
                for k in range(TOPK):
                    last = dve.tensor_scalar(oneh[:, n, k, :], iota[:, 0:NE], top_f[:, k:k + 1], None, ALU.is_equal)
                link(last)
                dve.tensor_reduce(chosen[:, n, :], oneh[:, n].rearrange("p k e -> p e k"), AX.X, ALU.add).then_inc(s_ch, 1)

            dve.wait_ge(s_g1c, 1)
            gate_o(0)
            for n in range(NT):
                if n + 1 < NT:
                    gate_o(n + 1)
                dve.wait_ge(s_yr, n + 1)
                link(dve.reciprocal(rst[:, 10:11], rst[:, 8:9]))
                if n >= 2:
                    dve.wait_ge(s_x1s[n % 2], 16 * (n // 2))
                link(dve.scalar_tensor_tensor(x1[:, n % 2, :], ps[:, 2:4, :].rearrange("p b c -> p (b c)"),
                                              rst[:, 10:11], g1row, ALU.mult, ALU.mult))
                dve.wait_ge(s_xr[n % 2], 16 * (n // 2 + 1))
                dve.tensor_tensor(x1[:, n % 2, :], x1[:, n % 2, :], xr[:, n % 2, :], ALU.add).then_inc(s_x1, 1)
                if n >= 1:
                    route(n - 1)
                dve.wait_ge(s_x1r, n + 1)
                link(dve.reciprocal(rst[:, 11:12], rst[:, 9:10]))
                if n >= 2:
                    dve.wait_ge(s_n2s[n % 2], 16 * (n // 2))
                    dve.wait_ge(s_n2T, n - 1)
                dve.tensor_scalar(xn2[:, n % 2, :], x1[:, n % 2, :], rst[:, 11:12], None, ALU.mult).then_inc(s_n2, 1)
                dve.wait_ge(s_n2T, n + 1)
                for k in range(4):
                    last = dve.tensor_scalar(h2T[:, n % 2, k, :], ps[:, 4, k * P:(k + 1) * P],
                                             sc2[:, k:k + 1], modc[:, 24 + k, 0:1], ALU.mult, ALU.add)
                last.then_inc(s_h2V, 1)
            route(NT - 1)

            link(dve.tensor_tensor(strict[:], tri[0:NE, 0, 0:NE], ident[0:NE, 0:NE], ALU.subtract))
            dve.wait_ge(s_cnt, 1)
            link(dve.tensor_scalar(nbf[:], ps[0:NE, 1, 0:1], float(P - 1), None, ALU.add))
            link(dve.tensor_copy(nbi[:], nbf[:]))
            link(dve.tensor_single_scalar(nbi[:], nbi[:], 7, ALU.logical_shift_right))
            link(dve.tensor_copy(nbf[:], nbi[:]))
            dve.sem_inc(s_nb, 1)
            dve.wait_ge(s_cum, 1)
            link(dve.tensor_copy(endf[:], ps[0:NE, 2, 0:1]))
            link(dve.tensor_scalar(past, iota[0:NE, 0:64], endf[:, 0:1], None, ALU.is_ge))
            dve.sem_inc(s_past, 1)
            link(dve.tensor_copy(base, ps[:, 3, 0:NE]))
            dve.wait_ge(s_exp, 1)
            link(dve.memset(meta_f, 1.0))
            link(dve.tensor_scalar(meta_f[:, 0:64], ps[0:1, 4, 0:64], float(NE - 1), None, ALU.min))
            link(dve.tensor_tensor(meta_f[:, 65:128], meta_f[:, 1:64], meta_f[:, 0:63], ALU.not_equal))
            link(dve.tensor_copy(meta_f[:, 128:129], ps[0:1, 5, 0:1]))
            link(dve.tensor_copy(meta, meta_f))
            dve.sem_inc(s_meta, 1)
            dve.wait_ge(s_rank, 1)
            rank = ps[:, 0, 0:NT * NE].rearrange("p (n e) -> p n e", n=NT)
            link(dve.tensor_tensor(chosen, rank, chosen, ALU.subtract))
            link(dve.scalar_tensor_tensor(chosen, base.unsqueeze(1).to_broadcast([P, NT, NE]), float(P), chosen,
                                          ALU.mult, ALU.add))
            work = HT[:, 0:NT * TOPK * NE].rearrange("p (n k e) -> p n k e", n=NT, k=TOPK)
            for n in range(NT):
                last = dve.tensor_tensor(work[:, n], oneh[:, n], chosen[:, n, :].unsqueeze(1).to_broadcast([P, TOPK, NE]),
                                         ALU.mult)
            link(last)
            link(dve.tensor_reduce(dests, work, AX.X, ALU.add))
            link(dve.tensor_copy(dest_i.rearrange("p (n k) -> p n k", n=NT), dests))
            link(dve.tensor_single_scalar(tmp_i, dest_i, P - 1, ALU.bitwise_and))
            link(dve.tensor_copy(slotf, tmp_i))
            link(dve.tensor_single_scalar(tmp_i, dest_i, 7, ALU.logical_shift_right))
            link(dve.tensor_copy(blkf, tmp_i))
            for m in range(NT * TOPK):
                if m >= 2:
                    dve.wait_ge(s_hotu, m - 1)
                dve.tensor_scalar(hotS[:, m % 2, :], iota[:], slotf[:, m:m + 1], None, ALU.is_equal)
                dve.tensor_scalar(hotB[:, m % 2, :], iota[:, 0:64], blkf[:, m:m + 1], tokid[:, m // TOPK:m // TOPK + 1],
                                  ALU.is_equal, ALU.mult).then_inc(s_hot, 1)
            dve.wait_ge(s_hotu, NT * TOPK)
            for i in range(2):
                dve.wait_ge(s_x1s[i], 16 * NT // 2)
                dve.wait_ge(s_n2s[i], 16 * NT // 2)
            dve.wait_ge(s_b3s, 16)
            link(dve.tensor_copy(slots, ps[:, 6, 0:64]))
            dve.sem_inc(s_slot, 1)
            link(dve.tensor_tensor(gates, top[:, :, 0:TOPK], top[:, :, 0:1].to_broadcast([P, NT, TOPK]), ALU.subtract))
            dve.sem_inc(s_sm, 1)
            dve.wait_ge(s_sm, 2)
            link(dve.tensor_reduce(slotf[:, 0:NT], gates, AX.X, ALU.add))
            link(dve.reciprocal(slotf[:, 0:NT], slotf[:, 0:NT]))
            link(dve.tensor_tensor(gates, gates, slotf[:, 0:NT].unsqueeze(2).to_broadcast([P, NT, TOPK]), ALU.mult))
            link(dve.memset(onesb[0:3, :], 1.0))

            nblk = dve.value_load(meta[0:1, 128:129], min_val=SEQ * TOPK // P, max_val=MAXB)
            for e in (e_xv, e_g, e_act):
                e.ahead(dve)

            def xT_half():
                for k in range(4):
                    last = dve.tensor_scalar(xT[:, k, :], ps[:, 0, k * P:(k + 1) * P],
                                             sc2[:, k:k + 1], modc[:, 24 + k, 0:1], ALU.mult, ALU.add)
                last.then_inc(e_xv.sem, 1)

            dve.wait_ge(e_xgT.sem, 2)
            xT_half()
            with dve.Fori(0, MAXB) as t:
                with dve.If(t < nblk):
                    link.turn(t, 12)
                    for j in range(4):
                        gu = ps[:, 2 + j % 2, :].rearrange("p (f b) -> p f b", b=2)
                        g, u, a = gate_n[:, j % 2, :], up_n[:, j % 2, :], act_n[:, j % 2, :]
                        e_gu.now(dve, t, j)
                        dve.tensor_scalar(g, gu[:, :, 0], LIMIT, None, ALU.min).then_inc(e_g.sem, 1)
                        link(dve.tensor_scalar(u, gu[:, :, 1], LIMIT, -LIMIT, ALU.min, ALU.max))
                        e_g.now(dve, t, j)
                        link(dve.scalar_tensor_tensor(u, u, 1.0, g, ALU.add, ALU.mult))
                        e_sg.now(dve, t, j)
                        if j >= 2:
                            e_aT.now(dve, t, j - 2)
                        else:
                            e_aT.before(dve, t, j + 2)
                        link(dve.tensor_tensor(a, u, sig_n[:, j % 2, :], ALU.mult))
                        dve.sem_inc(e_act.sem, 1)
                    dve.wait_ge(e_xgT.sem, t + 3)
                    xT_half()
            link2 = Link(dve, s_dve2)

            oh = oneh
            for n in range(NT):
                for k in range(TOPK):
                    if k == 0:
                        link2(dve.tensor_scalar(mixe[:, n, :], oh[:, n, k, :], gates[:, n, k:k + 1], None, ALU.mult))
                    else:
                        link2(dve.scalar_tensor_tensor(mixe[:, n, :], oh[:, n, k, :], gates[:, n, k:k + 1],
                                                       mixe[:, n, :], ALU.mult, ALU.add))
            dve.sem_inc(s_mixe, 1)
            dve.wait_ge(s_g2c, 1)
            for n in range(NT):
                dve.wait_ge(s_bd, n + 1)
                dve.wait_ge(s_yg[n % 2], 64 * (n // 2 + 1))
                if n >= 1:
                    dve.wait_ge(s_accr, n)
                for k in range(TOPK):
                    src = ps[:, 3:5, :].rearrange("p b c -> p (b c)") if k == 0 else acc
                    link2(dve.scalar_tensor_tensor(acc, yg[:, n % 2, k, :], gates[:, n, k:k + 1], src, ALU.mult, ALU.add))
                dve.sem_inc(s_acc, 1)
                dve.wait_ge(s_accr, n + 1)
                link2(dve.reciprocal(rst[:, 1:2], rst[:, 0:1]))
                link2(dve.scalar_tensor_tensor(acc, acc, rst[:, 1:2], g2row, ALU.mult, ALU.mult))
                dve.wait_ge(s_x1l[n % 2], 16 * (n // 2 + 1))
                dve.tensor_tensor(x1r[:, n % 2, :], acc, x1r[:, n % 2, :], ALU.add).then_inc(s_fin, 1)

        @block.tensor
        def _(pe):
            pe.wait_ge(s_small, 80)
            pe.wait_ge(s_const, 1)
            pe.wait_ge(s_x[2], 16 * 7)
            pe.transpose(ps[:, 0, 0:96], rows[0:96, 0, :], ident[0:96, 0:96])
            pe.transpose(ps[:, 1, 0:36], rows[0:36, 1, :], ident[0:36, 0:36])
            for g in range(H):
                last = pe.transpose(ps[:, 2, g * P:(g + 1) * P], sgu_raw[:, g, :], ident[:])
            last.then_inc(s_colT, 1)

            def ada_cols(q):
                pe.wait_ge(s_adar, q + 1)
                if q >= 2:
                    pe.wait_ge(s_mod, q - 1)
                for a in range(4):
                    last = pe.transpose(ps[:, 2 + q % 2, 2 * a:2 * a + 2],
                                        modrow[0:2, q % 2, a * P:(a + 1) * P], ident[0:2, 0:2])
                last.then_inc(s_adaT, 1)

            pe.wait_ge(s_cs, 1)
            for q in range(NADA):
                pe.wait_ge(s_w[q % 3], 16 * (q // 3 + 1))
                if q >= 2:
                    pe.wait_ge(s_adar, q - 1)
                w = chunk(q)
                for k in range(KD):
                    last = pe.matmul(ps[0:2, q % 2, :], cs[:, k, :], w[:, k, :], start=k == 0, stop=k == KD - 1)
                last.then_inc(s_ada, 1)
                if q >= 1:
                    ada_cols(q - 1)
                    pe.sem_inc(s_wfree, 1)
            ada_cols(NADA - 1)
            pe.sem_inc(s_wfree, 1)

            pe.wait_ge(s_modA, 1)
            for i in range(NA):
                pe.wait_ge(s_xn, i + 1)
                if i >= 2:
                    pe.wait_ge(s_hA, i - 1)
                    pe.wait_ge(s_hV, i - 1)
                for k in range(KD):
                    last = pe.transpose(ps[:, 2 * (i % 2) + k // 4, (k % 4) * P:(k % 4 + 1) * P],
                                        xs[:, 2 + i % 2, k * P:(k + 1) * P], ident[:])
                last.then_inc(s_xT, 1)

            pe.wait_ge(s_hA, NA)
            pe.wait_ge(s_hV, NA)
            pe.wait_ge(s_x[3], 16)
            for n in range(NA):
                for k in range(KD):
                    last = pe.matmul(ps[:, 0, n * BA:(n + 1) * BA], hT[:, k, n * P:(n + 1) * P], wba[:, k, :],
                                     start=k == 0, stop=k == KD - 1)
            last.then_inc(s_pj, 1)

            def free(g):
                if g >= 6:
                    pe.wait_ge(s_pjf, g - 5)

            def loaded(q):
                pe.wait_ge(s_w[q % 3], 16 * (q // 3 + 1))

            def columns(g, q, ct, t0, n):
                free(g)
                w = chunk(q)
                for k in range(KD):
                    last = pe.matmul(ps[:, g % 6, 0:n], w[:, k, ct * P:(ct + 1) * P], hT[:, k, t0:t0 + n],
                                     start=k == 0, stop=k == KD - 1)
                last.then_inc(s_pj, 1)

            def natural(g, q, n):
                free(g)
                w = chunk(q)
                t0 = CTX + n * P
                for k in range(KD):
                    last = pe.matmul(ps[:, g % 6, :], hT[:, k, t0:t0 + P], w[:, k, :], start=k == 0, stop=k == KD - 1)
                last.then_inc(s_pj, 1)

            loaded(NADA)
            for g in range(G_U, G_V):
                columns(g, NADA, (g - G_U) // 2, CTX + 512 * ((g - G_U) % 2), 512)
            pe.wait_ge(s_pj, G_V)
            pe.sem_inc(s_wfree, 1)

            def spatial(n):
                pe.wait_ge(s_vn, n + 1)
                if n >= 2:
                    pe.wait_ge(s_sgf, n - 1)
                for g in range(H):
                    last = pe.matmul(ps[:, 6 + n % 2, g * P:(g + 1) * P], v_norm[:, n % 2, g * P:(g + 1) * P],
                                     sguT[:, g, :], start=True, stop=True)
                last.then_inc(s_sg, 1)

            loaded(NADA + 1)
            for g in range(G_V, G_Z):
                natural(g, NADA + 1, g - G_V)
                if g - G_V >= 2:
                    spatial(g - G_V - 2)
            pe.wait_ge(s_pj, G_Z)
            pe.sem_inc(s_wfree, 1)
            loaded(NADA + 2)
            for g in range(G_Z, G_QKV):
                natural(g, NADA + 2, g - G_Z)
                if g - G_Z < 2:
                    spatial(g - G_Z + NT - 2)
            pe.wait_ge(s_pj, G_QKV)
            pe.sem_inc(s_wfree, 1)
            for m in range(NG - G_QKV):
                ct = m // 3
                if m % 12 == 0:
                    if m:
                        pe.wait_ge(s_pj, G_QKV + m)
                        pe.sem_inc(s_wfree, 1)
                    loaded(NADA + 3 + ct // 4)
                columns(G_QKV + m, NADA + 3 + ct // 4, ct % 4, *SPANS[m % 3])
            for m in range(24):
                n = SPANS[m % 3][1]
                pe.wait_ge(s_sq, m + 1)
                if m >= 2:
                    pe.wait_ge(s_nrm, m - 1)
                if m == 0:
                    pe.wait_ge(s_pjf, NG)
                pe.matmul(ps[:, m % 2, 0:n], ones[:], conv_in[:, m % 2, 0:n], start=True, stop=True).then_inc(s_ss, 1)

            for e in (e_G, e_K, e_Q, e_P, e_TP, e_X, e_u, e_ws, e_o):
                e.ahead(pe)

            def heads(out, lhsT, rhs):
                for h in range(H):
                    last = pe.matmul(out[:, h, :], lhsT(h), rhs(h), start=True, stop=True)
                return last

            def turn(s, out):
                for r in range(DIRS):
                    e_st.now(pe, s, r)
                    e_S.before(pe, s, r)
                    heads(bank(r, 0), lambda h: gst[:, r, h:h + 1].to_broadcast([P, P]), lambda h: tri[:, r, :])
                    small = bank(r, 3)[:, 0, :]
                    pe.matmul(small[:, 0:4], tri[:, r, :], gst[:, r, :], start=True, stop=True)
                    pe.matmul(small[:, 4:8], ones[:], gst[:, r, :], start=True, stop=True).then_inc(e_G.sem, 1)
                for r in range(DIRS):
                    kc = dn[r]["kc"]
                    heads(bank(r, 1), lambda h: bst[:, r, h:h + 1].to_broadcast([P, P]), lambda h: ident[:])
                    heads(bank(r, 2), lambda h: kc[:, h, :], lambda h: kc[:, h, :]).then_inc(e_K.sem, 1)
                for r in range(DIRS):
                    d = dn[r]
                    e_E.now(pe, s, r)
                    e_D.now(pe, s, r)
                    if out:
                        heads(bank(r, 3), lambda h: d["kc"][:, h, :], lambda h: d["qc"][:, h, :])
                    for h in range(H):
                        pe.transpose(bank(r, 0)[:, h, :], d["kc"][:, h, :], ident[:])
                    e_A.now(pe, s, r)
                    for h in range(H):
                        last = pe.transpose(bank(r, 1)[:, h, :], d["vc"][:, h, :], ident[:])
                    last.then_inc(e_Q.sem, 1)
                for l in range(LEVELS):
                    if l >= 1:
                        for r in range(DIRS):
                            d = dn[r]
                            if l == 1:
                                e_KV.now(pe, s, r)
                            e_B.now(pe, s, 2 * l + r)
                            e_Xc.now(pe, s, 2 * (l - 1) + r)
                            b = d["b%d" % (l % 2)]
                            heads(bank(r, 0), lambda h: b[:, h, :], lambda h: d["t"][:, h, :]).then_inc(e_P.sem, 1)
                        for r in range(DIRS):
                            d = dn[r]
                            e_Pc.now(pe, s, 2 * (l - 1) + r)
                            heads(bank(r, 1), lambda h: d["prod"][:, h, :],
                                  lambda h: d["tT"][:, h, :]).then_inc(e_TP.sem, 1)
                    if l < NL:
                        for r in range(DIRS):
                            d = dn[r]
                            e_T.now(pe, s, 2 * l + r)
                            for h in range(H):
                                last = pe.transpose(bank(r, 2)[:, h, :], d["tT"][:, h, :], ident[:])
                            last.then_inc(e_X.sem, 1)
                for r in range(DIRS):
                    d = dn[r]
                    e_T.now(pe, s, 2 * NL + r)
                    heads(bank(r, 1), lambda h: d["kbg"][:, h, :], lambda h: d["tT"][:, h, :])
                    heads(bank(r, 0), lambda h: d["tT"][:, h, :], lambda h: d["vb"][:, h, :]).then_inc(e_u.sem, 1)
                for r in range(DIRS):
                    d = dn[r]
                    e_uc.now(pe, s, r)
                    heads(bank(r, 2), lambda h: d["wT"][:, h, :], lambda h: d["state"][:, h, :]).then_inc(e_ws.sem, 1)
                for r in range(DIRS):
                    d = dn[r]
                    if out:
                        e_qd.now(pe, s, r)
                    e_vn.now(pe, s, r)
                    if out:
                        for h in range(H):
                            pe.matmul(bank(r, 0)[:, h, :], d["qd"][:, h, :], d["state"][:, h, :], start=True, stop=False)
                            pe.matmul(bank(r, 0)[:, h, :], d["attnT"][:, h, :], d["vnew"][:, h, :], start=False, stop=True)
                    heads(bank(r, 3), lambda h: d["kdec"][:, h, :], lambda h: d["vnew"][:, h, :]).then_inc(e_o.sem, 1)

            deltanet(pe, turn)

            def spread_row(banks, v):
                for k in range(KD):
                    last = pe.matmul(ps[:, banks + k // 4, (k % 4) * P:(k % 4 + 1) * P],
                                     gvec[:, v, k:k + 1].to_broadcast([P, P]), ident[:], start=True, stop=True)
                return last

            pe.wait_ge(s_ogate, 1)
            spread_row(6, 0).then_inc(s_g1, 1)
            pe.wait_ge(s_g1c, 1)
            pe.wait_ge(s_rw, 32)

            def turn_o(n):
                pe.wait_ge(s_on, n + 1)
                if n >= 2:
                    pe.wait_ge(s_mx, n - 1)
                for h in range(H):
                    last = pe.transpose(ps[:, n % 2, h * P:(h + 1) * P], on[:, n % 2, h * P:(h + 1) * P], ident[:])
                last.then_inc(s_oT, 1)

            def router(n):
                pe.wait_ge(s_n2, n + 1)
                if n >= 1:
                    pe.wait_ge(s_h2A, n)
                    pe.wait_ge(s_h2V, n)
                for k in range(KD):
                    last = pe.transpose(ps[:, 4 + k // 4, (k % 4) * P:(k % 4 + 1) * P],
                                        xn2[:, n % 2, k * P:(k + 1) * P], ident[:])
                last.then_inc(s_n2T, 1)
                pe.wait_ge(s_h2A, n + 1)
                pe.wait_ge(s_h2V, n + 1)
                if n >= 1:
                    pe.wait_ge(s_lg, n)
                for k in range(KD):
                    last = pe.matmul(ps[:, 6, 0:NE], h2T[:, n % 2, k, :], rw[:, k, :], start=k == 0, stop=k == KD - 1)
                last.then_inc(s_rt2, 1)

            turn_o(0)
            for n in range(NT):
                if n + 1 < NT:
                    turn_o(n + 1)
                pe.wait_ge(s_mx, n + 1)
                if n >= 1:
                    pe.wait_ge(s_x1, n)
                for i in range(2):
                    if n == 0:
                        pe.wait_ge(s_wo[i], 16)
                    for k in range(KD):
                        lhsT = mixT[:, n % 2, k, :] if k < H else uT[:, k - H, n * P:(n + 1) * P]
                        last = pe.matmul(ps[:, 2 + i, :], lhsT, wo[i][:, k, :], start=k == 0, stop=k == KD - 1)
                last.then_inc(s_y, 1)
                router(n)

            pe.wait_ge(s_ch, NT)
            for n in range(NT):
                last = pe.matmul(ps[0:NE, 1, 0:1], chosen[:, n, :], ones[:, 0:1], start=n == 0, stop=n == NT - 1)
            last.then_inc(s_cnt, 1)
            for n in range(NT):
                dst = ps[:, 0, n * NE:(n + 1) * NE]
                for j in range(n):
                    pe.matmul(dst, ones[:], chosen[:, j, :], start=j == 0, stop=False)
                last = pe.matmul(dst, tri[:, 0, :], chosen[:, n, :], start=n == 0, stop=True)
            last.then_inc(s_rank, 1)
            pe.wait_ge(s_nb, 1)
            pe.matmul(ps[0:NE, 2, 0:1], tri[0:NE, 0, 0:NE], nbf[:], start=True, stop=True)
            pe.matmul(ps[0:1, 5, 0:1], nbf[:], ones[0:NE, 0:1], start=True, stop=True)
            pe.matmul(ps[:, 3, 0:NE], nbf[:, 0:1].to_broadcast([NE, P]), strict[:], start=True, stop=True).then_inc(s_cum, 1)
            pe.wait_ge(s_past, 1)
            pe.matmul(ps[0:1, 4, 0:64], ones[0:NE, 0:1], past, start=True, stop=True).then_inc(s_exp, 1)
            M = NT * TOPK
            for m in range(M):
                pe.wait_ge(s_hot, m + 1)
                pe.matmul(ps[:, 6, 0:64], hotS[:, m % 2, :], hotB[:, m % 2, :], start=m == 0, stop=m == M - 1).then_inc(s_hotu, 1)

            nblk = pe.value_load(meta_wait(pe), min_val=SEQ * TOPK // P, max_val=MAXB)
            for e in (e_xgT, e_gu, e_aT, e_dn):
                e.ahead(pe)

            def turn_x():
                for k in range(KD):
                    last = pe.transpose(ps[:, k // 4, (k % 4) * P:(k % 4 + 1) * P], xg[:, k * P:(k + 1) * P], ident[:])
                last.then_inc(e_xgT.sem, 1)

            pe.wait_ge(s_slot, 1)
            pe.wait_ge(e_xg.sem, 16)
            turn_x()
            with pe.Fori(0, MAXB) as t:
                with pe.If(t < nblk):
                    def gate_up(j):
                        w = slot(j).rearrange("p (k n) -> p k n", k=KD)
                        if j >= 2:
                            e_act.now(pe, t, j - 2)
                        else:
                            e_act.before(pe, t, j + 2)
                        e_w[j].now(pe, t, 15)
                        for k in range(KD):
                            if k == 0 and j == 0:
                                e_xa.now(pe, t, 0)
                                e_xv.now(pe, t, 0)
                            pe.matmul(ps[:, 2 + j % 2, :], xT[:, k, :], w[:, k, :], start=k == 0, stop=False)
                        if j == 0:
                            e_b3.now(pe, t, 15)
                        pe.matmul(ps[:, 2 + j % 2, :], onesb[0:3, :], bias3[0:3, j * 512:(j + 1) * 512], start=False,
                                  stop=True).then_inc(e_gu.sem, 1)

                    def turn_act(j):
                        e_act.now(pe, t, j)
                        if j >= 2:
                            e_aTc.now(pe, t, j - 2)
                        else:
                            e_aTc.before(pe, t, j + 2)
                        for i in range(2):
                            last = pe.transpose(ps[:, 4 + 3 * (j % 2), i * P:(i + 1) * P], act_n[:, j % 2, i * P:(i + 1) * P], ident[:])
                        last.then_inc(e_aT.sem, 1)

                    def down(i, ks):
                        w = slot(4 + i).rearrange("p (k n) -> p k n", k=KD)
                        for k in ks:
                            if i == 0 and k % 2 == 0:
                                e_aTc.now(pe, t, k // 2)
                            last = pe.matmul(ps[:, 5 + i, :], actT[:, k, :], w[:, k, :], start=k == 0, stop=k == KD - 1)
                        return last

                    gate_up(0)
                    for j in range(1, 4):
                        gate_up(j)
                        turn_act(j - 1)
                    pe.wait_ge(e_xg.sem, 16 * t + 32)
                    turn_x()
                    e_w[4].now(pe, t, 15)
                    e_yc.before(pe, t, 1)
                    down(0, range(6))
                    turn_act(3)
                    down(0, range(6, 8)).then_inc(e_dn.sem, 1)
                    e_w[5].now(pe, t, 15)
                    down(1, range(8)).then_inc(e_dn.sem, 1)

            pe.wait_ge(e_xa.sem, nblk + 2)
            pe.wait_ge(e_xv.sem, nblk + 2)
            spread_row(0, 1).then_inc(s_g2, 1)
            pe.wait_ge(s_mixe, 1)
            pe.wait_ge(s_bdn, 16)
            for n in range(NT):
                if n >= 1:
                    pe.wait_ge(s_gTc, n)
                pe.transpose(ps[0:NE, 2, 0:P], mixe[:, n, :], ident[:]).then_inc(s_gT, 1)
                pe.wait_ge(s_gTc, n + 1)
                if n >= 1:
                    pe.wait_ge(s_acc, n)
                for i in range(2):
                    last = pe.matmul(ps[:, 3 + i, :], gT[0:NE, :], bdn[0:NE, i * 512:(i + 1) * 512], start=True, stop=True)
                last.then_inc(s_bd, 1)


_INS = ["x", "c", "ctx", "c_ctx", "w_ada", "b_ada", "norm_g", "w_in", "conv_w", "a_log", "dt_bias", "gdn_norm_g",
        "sgu_ln_g", "sgu_ln_b", "sgu_w", "sgu_b", "w_out", "router_w", "router_b", "w_gu", "b_gu", "w_down", "b_down"]
DBG = [None]


def kernel(**inputs):
    import numpy as _np
    import concourse.bacc as _bacc
    from concourse import mybir as _mybir
    from concourse.bass_utils import run_bass_kernel_spmd as _run

    nc = _bacc.Bacc("TRN2", target_bir_lowering=False, num_devices=1)
    arrays, args = {}, []
    for name in _INS:
        a = _np.ascontiguousarray(inputs[name])
        arrays[f"in_{name}_dram"] = a
        args.append(nc.dram_tensor(f"in_{name}_dram", a.shape, _mybir.dt.from_np(a.dtype), kind="ExternalInput").ap())
    out = nc.dram_tensor("out_0_dram", (1, 1024, 1024), _mybir.dt.float32, kind="ExternalOutput").ap()
    if DBG[0]:
        hybrid_block(nc, *args, out, dbg=nc.dram_tensor("dbg", DBG[0], _mybir.dt.float32, kind="ExternalOutput").ap())
    else:
        hybrid_block(nc, *args, out)
    r = _run(nc, [arrays], core_ids=[0])
    return r.results[0]["out_0_dram"]
```
